# Optimizing a Trainium2 kernel written in Bass

```python
import math
import jax, jax.numpy as jnp
from jax import lax
import numpy as np

D_MODEL = 1024
BATCH = 1
SEQ = 256
DEPTH = 2

N_MIXERS = 2
N_A = (DEPTH + 1) // 2
N_B = DEPTH // 2

CHUNK = 128
A_WIDTH = D_MODEL
A_GROUPS = 8
A_GROUP_DIM = A_WIDTH // A_GROUPS

N_HEADS = 8
HEAD_DIM = D_MODEL // N_HEADS // 2
V_HEAD_DIM = 2 * HEAD_DIM
QK_WIDTH = N_HEADS * 2 * HEAD_DIM
V_WIDTH = N_HEADS * V_HEAD_DIM
Q_BLOCK = 128
ROT_DIM = HEAD_DIM // 4
ROPE_THETA = 500000.0

D_FF = 4 * D_MODEL

PLE_DIM = 256
MAX_POS_OFFSET = 4096

RMS_EPS = 1e-6
LN_EPS = 1e-5
SUBLN_EPS = 1e-5


def _rmsnorm(x, g, eps=RMS_EPS):
    xf = x.astype(jnp.float32)
    y = xf * lax.rsqrt(jnp.mean(xf * xf, axis=-1, keepdims=True) + eps)
    return (y * g.astype(jnp.float32)).astype(x.dtype)

def _layernorm(x, g, b):
    xf = x.astype(jnp.float32)
    mu = jnp.mean(xf, axis=-1, keepdims=True)
    var = jnp.mean(jnp.square(xf - mu), axis=-1, keepdims=True)
    y = (xf - mu) * lax.rsqrt(var + LN_EPS)
    return (y * g.astype(jnp.float32) + b.astype(jnp.float32)).astype(x.dtype)

def _rotary_tables(positions, dtype):
    inv_freq = ROPE_THETA ** (-(jnp.arange(0, ROT_DIM, 2, dtype=jnp.float32) / ROT_DIM))
    ang = positions.astype(jnp.float32)[..., None] * inv_freq
    cos = jnp.cos(ang)[:, :, None, None, :].astype(dtype)
    sin = jnp.sin(ang)[:, :, None, None, :].astype(dtype)
    return cos, sin

def _partial_rotary(x, cos, sin):
    xr, xp = x[..., :ROT_DIM], x[..., ROT_DIM:]
    x1, x2 = jnp.split(xr, 2, axis=-1)
    return jnp.concatenate([x1 * cos - x2 * sin, x2 * cos + x1 * sin, xp], axis=-1)

def _chunked_gmlp(a, w_in, ln_g, ln_b, w_s, b_s, w_out):
    B, S, _ = a.shape
    z = jax.nn.gelu(a @ w_in)
    u, v = jnp.split(z, 2, axis=-1)
    v = _layernorm(v, ln_g, ln_b)
    v = v.reshape(B, S // CHUNK, CHUNK, A_GROUPS, A_GROUP_DIM)
    w_causal = w_s * jnp.tril(jnp.ones((CHUNK, CHUNK), dtype=w_s.dtype))
    s = jnp.einsum('gts,bnsgd->bntgd', w_causal, v) + b_s.T[:, :, None]
    y = u * s.reshape(B, S, A_WIDTH)
    return y @ w_out

def _diff_attention(a, positions, w_qkv, lam_q1, lam_k1, lam_q2, lam_k2, subln_g, w_o, lambda_init):
    B, S, _ = a.shape
    qkv = a @ w_qkv
    q, k, v = jnp.split(qkv, [QK_WIDTH, 2 * QK_WIDTH], axis=-1)
    q = q.reshape(B, S, N_HEADS, 2, HEAD_DIM)
    k = k.reshape(B, S, N_HEADS, 2, HEAD_DIM)
    v = v.reshape(B, S, N_HEADS, V_HEAD_DIM)
    cos, sin = _rotary_tables(positions, q.dtype)
    q = _partial_rotary(q, cos, sin)
    k = _partial_rotary(k, cos, sin)
    f32 = jnp.float32
    lam = (jnp.exp(jnp.sum(lam_q1.astype(f32) * lam_k1.astype(f32)))
           - jnp.exp(jnp.sum(lam_q2.astype(f32) * lam_k2.astype(f32))) + lambda_init)
    scale = HEAD_DIM ** -0.5
    outs = []
    for blk in range(S // Q_BLOCK):
        q0 = blk * Q_BLOCK
        q1 = q0 + Q_BLOCK
        qb = q[:, q0:q1]
        kb = k[:, :q1]
        vb = v[:, :q1]
        sc = jnp.einsum('bqhcd,bkhcd->bhcqk', qb, kb).astype(f32) * scale
        mask = (q0 + jnp.arange(Q_BLOCK))[:, None] >= jnp.arange(q1)[None, :]
        sc = jnp.where(mask, sc, -jnp.inf)
        pr = jax.nn.softmax(sc, axis=-1)
        attn = (pr[:, :, 0] - lam * pr[:, :, 1]).astype(vb.dtype)
        outs.append(jnp.einsum('bhqk,bkhe->bqhe', attn, vb))
    o = jnp.concatenate(outs, axis=1)
    o = _rmsnorm(o, subln_g, SUBLN_EPS) * (1.0 - lambda_init)
    return o.reshape(B, S, V_WIDTH) @ w_o

def _sqrelu_mlp(x, w_up, w_down):
    return jnp.square(jax.nn.relu(x @ w_up)) @ w_down

def first_inputs(seed: int = 0) -> dict:
    key = jax.random.key(seed)
    ks = jax.random.split(key, 32)
    f32 = jnp.float32

    def nrm(k, shape, scale):
        return jax.random.normal(k, shape, f32) * scale

    def gain(k, shape):
        return 1.0 + 0.05 * jax.random.normal(k, shape, f32)

    x = nrm(ks[0], (BATCH, SEQ, D_MODEL), 1.0)
    p = nrm(ks[1], (DEPTH, BATCH, SEQ, PLE_DIM), 1.0)
    offsets = jax.random.randint(ks[2], (BATCH, 1), 0, MAX_POS_OFFSET, dtype=jnp.int32)
    positions = (offsets + jnp.arange(SEQ, dtype=jnp.int32)[None, :]).astype(jnp.int32)
    return {
        "x": x,
        "p": p,
        "positions": positions,
        "g_mix_pre": gain(ks[3], (DEPTH, D_MODEL)),
        "g_mix_post": gain(ks[4], (DEPTH, D_MODEL)),
        "g_ffn_pre": gain(ks[5], (DEPTH, D_MODEL)),
        "g_ffn_post": gain(ks[6], (DEPTH, D_MODEL)),
        "g_ple_pre": gain(ks[7], (DEPTH, D_MODEL)),
        "g_ple_post": gain(ks[8], (DEPTH, D_MODEL)),
        "a_w_in": nrm(ks[9], (N_A, D_MODEL, 2 * A_WIDTH), D_MODEL ** -0.5),
        "a_ln_g": gain(ks[10], (N_A, A_WIDTH)),
        "a_ln_b": nrm(ks[11], (N_A, A_WIDTH), 0.02),
        "a_w_s": nrm(ks[12], (N_A, A_GROUPS, CHUNK, CHUNK), CHUNK ** -0.5),
        "a_b_s": 1.0 + nrm(ks[13], (N_A, A_GROUPS, CHUNK), 0.1),
        "a_w_out": nrm(ks[14], (N_A, A_WIDTH, D_MODEL), A_WIDTH ** -0.5),
        "b_w_qkv": nrm(ks[15], (N_B, D_MODEL, 2 * QK_WIDTH + V_WIDTH), D_MODEL ** -0.5),
        "b_lam_q1": nrm(ks[16], (N_B, HEAD_DIM), 0.1),
        "b_lam_k1": nrm(ks[17], (N_B, HEAD_DIM), 0.1),
        "b_lam_q2": nrm(ks[18], (N_B, HEAD_DIM), 0.1),
        "b_lam_k2": nrm(ks[19], (N_B, HEAD_DIM), 0.1),
        "b_subln_g": gain(ks[20], (N_B, V_HEAD_DIM)),
        "b_w_o": nrm(ks[21], (N_B, V_WIDTH, D_MODEL), V_WIDTH ** -0.5),
        "f_w_up": nrm(ks[22], (DEPTH, D_MODEL, D_FF), D_MODEL ** -0.5),
        "f_w_down": nrm(ks[23], (DEPTH, D_FF, D_MODEL), D_FF ** -0.5),
        "ple_w_proj": nrm(ks[24], (DEPTH, PLE_DIM, D_MODEL), PLE_DIM ** -0.5),
        "ple_w_gate": nrm(ks[25], (DEPTH, D_MODEL, D_MODEL), D_MODEL ** -0.5),
        "ple_b_gate": nrm(ks[26], (DEPTH, D_MODEL), 0.02),
    }

def first_block(x, p, positions, g_mix_pre, g_mix_post, g_ffn_pre, g_ffn_post, g_ple_pre, g_ple_post,
              a_w_in, a_ln_g, a_ln_b, a_w_s, a_b_s, a_w_out,
              b_w_qkv, b_lam_q1, b_lam_k1, b_lam_q2, b_lam_k2, b_subln_g, b_w_o,
              f_w_up, f_w_down, ple_w_proj, ple_w_gate, ple_b_gate):
    h = x
    for i in range(DEPTH):
        j = i // N_MIXERS
        a = _rmsnorm(h, g_mix_pre[i])
        if i % N_MIXERS == 0:
            m = _chunked_gmlp(a, a_w_in[j], a_ln_g[j], a_ln_b[j], a_w_s[j], a_b_s[j], a_w_out[j])
        else:
            lambda_init = 0.8 - 0.6 * math.exp(-0.3 * i)
            m = _diff_attention(a, positions, b_w_qkv[j], b_lam_q1[j], b_lam_k1[j], b_lam_q2[j],
                                b_lam_k2[j], b_subln_g[j], b_w_o[j], lambda_init)
        h = h + _rmsnorm(m, g_mix_post[i])
        f = _sqrelu_mlp(_rmsnorm(h, g_ffn_pre[i]), f_w_up[i], f_w_down[i])
        h = h + _rmsnorm(f, g_ffn_post[i])
        gate = jax.nn.sigmoid(_rmsnorm(h, g_ple_pre[i]) @ ple_w_gate[i] + ple_b_gate[i])
        e = gate * (p[i] @ ple_w_proj[i])
        h = h + _rmsnorm(e, g_ple_post[i])
    return h


DEPTH_2 = 1

RET_HEADS = 4
RET_DK = 128
RET_DV = 256
RET_CHUNK = 128
SWA_HEADS = 8
SWA_KV_HEADS = 2
SWA_DH = 64
WINDOW = 128
D_FF_2 = 4 * D_MODEL
EPS = 1e-6

RET_QK = RET_HEADS * RET_DK
RET_V = RET_HEADS * RET_DV
SWA_Q = SWA_HEADS * SWA_DH
SWA_KV = SWA_KV_HEADS * SWA_DH
IN_SPLITS = (RET_QK, RET_QK, RET_V, RET_V, SWA_Q, SWA_KV, SWA_KV, D_MODEL, D_MODEL)
D_IN = sum(IN_SPLITS)
SPLIT_IDX = tuple(int(i) for i in np.cumsum(IN_SPLITS)[:-1])


def rmsnorm(x, g):
    xf = x.astype(jnp.float32)
    y = xf * lax.rsqrt(jnp.mean(xf * xf, axis=-1, keepdims=True) + EPS)
    return (y * g.astype(jnp.float32)).astype(x.dtype)

def retention_chunkwise(q, k, v):
    B, T, H, dk = q.shape
    dv = v.shape[-1]
    C = RET_CHUNK
    N = T // C
    f32 = jnp.float32
    log_gamma = jnp.log(1.0 - jnp.exp2(-5.0 - jnp.arange(H, dtype=f32)))
    q = q.astype(f32).reshape(B, N, C, H, dk)
    k = k.astype(f32).reshape(B, N, C, H, dk) * (dk ** -0.5)
    v = v.astype(f32).reshape(B, N, C, H, dv)
    pos = jnp.arange(C, dtype=f32)
    diff = pos[:, None] - pos[None, :]
    causal = diff >= 0
    decay = jnp.where(causal[None], jnp.exp(log_gamma[:, None, None] * jnp.where(causal, diff, 0.0)[None]), 0.0)
    qk = jnp.einsum('bnihd,bnjhd->bnhij', q, k) * decay[None, None]
    o_inner = jnp.einsum('bnhij,bnjhe->bnihe', qk, v)
    k_dec = k * jnp.exp(log_gamma[None, :] * (C - 1.0 - pos)[:, None])[None, None, :, :, None]
    kv = jnp.einsum('bnjhd,bnjhe->nbhde', k_dec, v)
    chunk_decay = jnp.exp(log_gamma * C)[None, :, None, None]

    def step(s, kv_n):
        return chunk_decay * s + kv_n, s

    _, s_prev = lax.scan(step, jnp.zeros((B, H, dk, dv), f32), kv)
    q_dec = q * jnp.exp(log_gamma[None, :] * (pos + 1.0)[:, None])[None, None, :, :, None]
    o_cross = jnp.einsum('bnihd,nbhde->bnihe', q_dec, s_prev)
    o = (o_inner + o_cross).reshape(B, T, H, dv)
    mu = jnp.mean(o, axis=-1, keepdims=True)
    var = jnp.mean(jnp.square(o - mu), axis=-1, keepdims=True)
    return (o - mu) * lax.rsqrt(var + EPS)

def swa_gqa_sinks(q, k, v, sinks):
    B, T, Hq, dh = q.shape
    G = k.shape[2]
    R = Hq // G
    W = WINDOW
    N = T // W
    f32 = jnp.float32
    qb = q.reshape(B, N, W, G, R, dh)
    kb = k.reshape(B, N, W, G, dh)
    vb = v.reshape(B, N, W, G, dh)
    pad = ((0, 0), (1, 0), (0, 0), (0, 0), (0, 0))
    kk = jnp.concatenate([jnp.pad(kb, pad)[:, :-1], kb], axis=2)
    vv = jnp.concatenate([jnp.pad(vb, pad)[:, :-1], vb], axis=2)
    s = jnp.einsum('bnigrd,bnjgd->bgrnij', qb, kk).astype(f32) * (dh ** -0.5)
    qpos = jnp.arange(W)[:, None] + W
    kpos = jnp.arange(2 * W)[None, :]
    dist = qpos - kpos
    valid = (dist >= 0) & (dist < W)
    blk_valid = valid[None] & ((jnp.arange(N)[:, None, None] > 0) | (kpos >= W)[None])
    slopes = jnp.exp2(-8.0 / Hq * jnp.arange(1, Hq + 1, dtype=f32)).reshape(G, R)
    s = s - slopes[None, :, :, None, None, None] * dist.astype(f32)[None, None, None, None]
    s = jnp.where(blk_valid[None, None, None], s, -jnp.inf)
    sink = sinks.astype(f32).reshape(G, R)[None, :, :, None, None, None]
    m = jnp.maximum(jnp.max(s, axis=-1, keepdims=True), sink)
    p = jnp.exp(s - m)
    p = p / (jnp.sum(p, axis=-1, keepdims=True) + jnp.exp(sink - m))
    out = jnp.einsum('bgrnij,bnjgd->bnigrd', p, vv.astype(f32))
    return out.reshape(B, T, Hq * dh)

def second_inputs(seed: int = 0) -> dict:
    key = jax.random.key(seed)
    ks = jax.random.split(key, 13)
    f32 = jnp.float32

    def dense(k, fan_in, fan_out):
        return jax.random.normal(k, (DEPTH_2, fan_in, fan_out), f32) * (fan_in ** -0.5)

    def gain(k):
        return 1.0 + 0.02 * jax.random.normal(k, (DEPTH_2, D_MODEL), f32)

    return {
        "x": jax.random.normal(ks[0], (BATCH, SEQ, D_MODEL), f32),
        "pre_mix_norm": gain(ks[1]),
        "w_in": dense(ks[2], D_MODEL, D_IN),
        "w_ret_out": dense(ks[3], RET_V, D_MODEL),
        "w_swa_out": dense(ks[4], SWA_Q, D_MODEL),
        "w_out": dense(ks[5], D_MODEL, D_MODEL),
        "sinks": 0.5 * jax.random.normal(ks[6], (DEPTH_2, SWA_HEADS), f32),
        "post_mix_norm": gain(ks[7]),
        "pre_mlp_norm": gain(ks[8]),
        "w_up": dense(ks[9], D_MODEL, D_FF_2),
        "w_down": dense(ks[10], D_FF_2, D_MODEL),
        "post_mlp_norm": gain(ks[11]),
    }

def second_block(x, pre_mix_norm, w_in, w_ret_out, w_swa_out, w_out, sinks, post_mix_norm, pre_mlp_norm, w_up, w_down, post_mlp_norm):
    B, T, _ = x.shape
    dt = x.dtype
    for l in range(DEPTH_2):
        h = rmsnorm(x, pre_mix_norm[l])
        proj = h @ w_in[l]
        q_r, k_r, v_r, g_r, q_s, k_s, v_s, gate_r, gate_s = jnp.split(proj, SPLIT_IDX, axis=-1)
        ret = retention_chunkwise(q_r.reshape(B, T, RET_HEADS, RET_DK),
                                  k_r.reshape(B, T, RET_HEADS, RET_DK),
                                  v_r.reshape(B, T, RET_HEADS, RET_DV)).reshape(B, T, RET_V)
        ret = (jax.nn.silu(g_r.astype(jnp.float32)) * ret).astype(dt)
        y_r = ret @ w_ret_out[l]
        swa = swa_gqa_sinks(q_s.reshape(B, T, SWA_HEADS, SWA_DH),
                            k_s.reshape(B, T, SWA_KV_HEADS, SWA_DH),
                            v_s.reshape(B, T, SWA_KV_HEADS, SWA_DH),
                            sinks[l]).astype(dt)
        y_s = swa @ w_swa_out[l]
        merged = jax.nn.sigmoid(gate_r) * y_r + jax.nn.sigmoid(gate_s) * y_s
        x = x + rmsnorm(merged @ w_out[l], post_mix_norm[l])
        h = rmsnorm(x, pre_mlp_norm[l])
        u = jnp.square(jax.nn.relu(h @ w_up[l]))
        x = x + rmsnorm(u @ w_down[l], post_mlp_norm[l])
    return x


def setup_inputs(seed=0):
    out = dict(first_inputs(seed))
    for name, value in second_inputs(seed + 1).items():
        if name != "x":
            out[name + "_2"] = value
    return out


def reference(
    x, p, positions, g_mix_pre, g_mix_post, g_ffn_pre, g_ffn_post, g_ple_pre, g_ple_post,
    a_w_in, a_ln_g, a_ln_b, a_w_s, a_b_s, a_w_out, b_w_qkv, b_lam_q1, b_lam_k1, b_lam_q2,
    b_lam_k2, b_subln_g, b_w_o, f_w_up, f_w_down, ple_w_proj, ple_w_gate, ple_b_gate,
    pre_mix_norm_2, w_in_2, w_ret_out_2, w_swa_out_2, w_out_2, sinks_2, post_mix_norm_2,
    pre_mlp_norm_2, w_up_2, w_down_2, post_mlp_norm_2,
):
    x = first_block(
        x, p, positions, g_mix_pre, g_mix_post, g_ffn_pre, g_ffn_post, g_ple_pre, g_ple_post,
        a_w_in, a_ln_g, a_ln_b, a_w_s, a_b_s, a_w_out, b_w_qkv, b_lam_q1, b_lam_k1, b_lam_q2,
        b_lam_k2, b_subln_g, b_w_o, f_w_up, f_w_down, ple_w_proj, ple_w_gate, ple_b_gate,
    )
    return second_block(
        x, pre_mix_norm_2, w_in_2, w_ret_out_2, w_swa_out_2, w_out_2, sinks_2, post_mix_norm_2,
        pre_mlp_norm_2, w_up_2, w_down_2, post_mlp_norm_2,
    )


_drawn_inputs = setup_inputs


def setup_inputs(seed=0):
    import zlib

    import numpy as np

    out = dict(_drawn_inputs(seed))
    spreads = {}
    factors = {'g_ple_pre': 4.175,
     'a_ln_g': 3.058,
     'a_ln_b': 7.265,
     'ple_b_gate': 8.0,
     'pre_mix_norm_2': 4.161,
     'sinks_2': 14.173,
     'post_mix_norm_2': 21.217,
     'pre_mlp_norm_2': 68.428,
     'post_mlp_norm_2': 99.488}
    for name, (base, spread) in spreads.items():
        noise = np.random.default_rng([zlib.crc32(name.encode()), seed]).standard_normal(out[name].shape)
        drawn = base * np.exp(spread * noise) if base else spread * noise
        out[name] = __import__('jax').numpy.asarray(drawn.astype(out[name].dtype))
    for name, factor in factors.items():
        out[name] = (out[name] * factor).astype(out[name].dtype)
    return out
```

```python
import math
from contextlib import ExitStack

import concourse.bass as bass
from concourse import mybir

F32 = mybir.dt.float32
F32R = mybir.dt.float32r
BF16 = mybir.dt.bfloat16
I32 = mybir.dt.int32
ALU = mybir.AluOpType
ACT = mybir.ActivationFunctionType
AX_X = mybir.AxisListType.X

P = 128
D = 1024
KT = D // P
TT = 2
SEQ = TT * P
TILE = 2048
RING = 4
LEAD = 3
BANK = 512
X, Y = 0, 4
GAINS = 3

T_V0, T_U0, T_OUT0, T_PROJ0, T_FFN0, T_GATE0 = 0, 4, 8, 12, 13, 45
T_Q, T_K, T_V, T_WO, T_PROJ1, T_FFN1, T_GATE1 = 49, 53, 57, 61, 65, 66, 98
T_VR, T_GR, T_QR, T_KR, T_QS, T_KVS, T_GATER, T_GATES = 102, 106, 110, 112, 114, 116, 117, 121
T_RET, T_SWA, T_OUT2, T_FFN2, T_END = 125, 129, 131, 135, 167
FFN_TILES = (T_FFN0, T_FFN1, T_FFN2)
FFN_CHUNKS = 8

C_PRE = {0: 0, 1: 9, 2: 13, 3: 18, 4: 26, 5: 30, 6: 34, 7: 48}
C_Y0, C_O1, C_SWA, C_RET, C_MERGED = 5, 22, (38, 43), 39, 44
C_P = {0: 4, 1: 17}

(A_V0, A_OUT0, A_PROJ0, A_FFN0, A_GATE0, A_Q, A_K, A_WO, A_PROJ1, A_FFN1, A_GATE1,
 A_VR, A_GR, A_GATER, A_GATES, A_YS, A_OUT2, A_FFN2) = range(18)

OUTPUTS = {1: 0, 2: 1, 4: 2, 5: 3, 7: 4, 8: 5}

(G_PRE0, G_LNG, G_LNB, G_POST0, G_FPRE0, G_FPOST0, G_PPRE0, G_BG0, G_PPOST0,
 G_PRE1, G_POST1, G_FPRE1, G_FPOST1, G_PPRE1, G_BG1, G_PPOST1,
 G_PRE2, G_POST2, G_FPRE2, G_FPOST2) = range(20)
GAIN_PRE = (G_PRE0, G_FPRE0, G_PPRE0, G_PRE1, G_FPRE1, G_PPRE1, G_PRE2, G_FPRE2)
GAIN_POST = (G_POST0, G_FPOST0, G_PPOST0, G_POST1, G_FPOST1, G_PPOST1, G_POST2, G_FPOST2)



def rms_order():
    order = []
    for j in range(9):
        for t in range(2):
            order += [("post", j, t)] * (j >= 1) + [("pre", j, t)] * (j <= 7)
    return {key: n for n, key in enumerate(order)}


RMS = rms_order()

HEADS = 8
ROT = 16
LAMBDA_INIT = 0.8 - 0.6 * math.exp(-0.3)
RET_HEADS, RET_DV = 4, 256
SWA_HEADS, SWA_DH = 8, 64
SLOPES = [2.0 ** (-8.0 / SWA_HEADS * (h + 1)) for h in range(SWA_HEADS)]
RMS_EPS, LN_EPS, SUBLN_EPS, RET_EPS = 1e-6, 1e-5, 1e-5, 1e-6
ROUND_MAGIC = 1.5 * 2.0 ** 23
TWO_PI_PARTS = (6.28125, 0.0019350051879882812, 3.0199159819567e-07)

K_ID, K_DIST, K_DECAY, K_TRIU, K_FREQ, K_END = 0, 128, 512, 1536, 1664, 1672


def build(nc, a, out):
    ctx = ExitStack()
    with ctx:
        def sb(name, shape, dt=F32):
            return ctx.enter_context(nc.sbuf_tensor(name, shape, dt))

        def sem(name):
            return ctx.enter_context(nc.semaphore(name))

        raw = sb("raw", [P, RING, TILE])
        high = sb("high", [P, RING, TILE], F32R)
        low = sb("low", [P, RING, TILE], F32R)
        h = sb("h", [P, TT, D])
        acth = sb("acth", [P, KT, SEQ], F32R)
        actl = sb("actl", [P, KT, SEQ], F32R)
        hidh = sb("hidh", [P, 2, BANK], F32R)
        hidl = sb("hidl", [P, 2, BANK], F32R)
        ph = sb("ph", [P, 2, SEQ], F32R)
        pl = sb("pl", [P, 2, SEQ], F32R)
        scratch = sb("scratch", [P, 1536])
        xn = sb("xn", [P, TT, D])
        junk = sb("junk", [P, 2, D], BF16)
        gain = sb("gain", [P, GAINS, D])
        cst = sb("cst", [P, K_END])
        ident16 = sb("ident16", [P, P], BF16)
        causal16 = sb("causal16", [P, P], BF16)
        ptok = sb("ptok", [P, TT, 256])
        arena = sb("arena", [P, 8448])
        ms = sb("ms", [P, 2, len(RMS)])
        rstd = sb("rstd", [P, len(RMS)])
        minus_half = sb("minus_half", [P, TT])
        bn = sb("bn", [P, 8, 12])
        mv = sb("mv", [P, 10, 2])
        mv_eps = sb("mv_eps", [P, 10])
        dev = sb("dev", [P, 10])
        o_ms = sb("o_ms", [P, 3, HEADS, TT])
        soft = sb("soft", [P, 2, 16])
        vecs = sb("vecs", [P, 392])
        sink8 = sb("sink8", [P, 8])
        lam = sb("lam", [P, 136])
        pos_i = sb("pos_i", [P, 2], I32)
        pos_f = sb("pos_f", [P, 2])
        trig_arg = sb("trig_arg", [P, 2, 2, 8])
        trig_n = sb("trig_n", [P, 2, 8])
        trig = sb("trig", [P, 2, 2, 8])
        ps = ctx.enter_context(nc.psum_tensor("ps", [P, 8, BANK], F32))

        relu = scratch[:, 0:1024].rearrange("p (b c) -> p b c", b=2)
        squared = scratch[:, 1024:1536]
        weighed = scratch[:, 0:1024].rearrange("p (b c) -> p b c", b=2)
        ident = cst[:, K_ID:K_ID + P]

        def flat(x):
            return x.rearrange("p a c -> p (a c)")

        def pair(x, t):
            return x[:, t, :].rearrange("p (b c) -> p b c", b=2)

        def half_of(x, t, b):
            return x[:, t, b * BANK:b * BANK + BANK]

        def h_halves(j, t, b):
            return 4 * (j - 1) + 2 * t + b + 1

        def acc_pair(acc, t):
            return ps[:, acc + 2 * t:acc + 2 * t + 2, :]

        def bank4(b):
            return ps[:, b, :].rearrange("p (k c) -> p k c", k=4)

        def act_part(x, t, b):
            return x[:, 4 * b:4 * b + 4, t * P:t * P + P]

        def xn_bank(b):
            return flat(xn[:, :, :])[:, b * BANK:b * BANK + BANK]

        def repeat(x, n):
            return x.unsqueeze(1).broadcast_to([P, n, x.shape[1]])

        v0 = arena[:, 0:2048].rearrange("p (t c) -> p t c", t=TT)
        proj = arena[:, 0:2048].rearrange("p (t c) -> p t c", t=TT)
        ut = arena[:, 2048:4096].rearrange("p (b c) -> p b c", b=4)
        ws_raw = arena[:, 4096:5120].rearrange("p (g c) -> p g c", g=8)
        wst = arena[:, 5120:6144].rearrange("p (g c) -> p g c", g=8)
        bs = arena[:, 6144:7168].rearrange("p (g c) -> p g c", g=8)
        qtok = arena[:, 0:2048].rearrange("p (t c) -> p t c", t=TT)
        qt = arena[:, 2048:4096].rearrange("p (h c) -> p h c", h=HEADS)
        kt_ = arena[:, 4096:6144].rearrange("p (h c) -> p h c", h=HEADS)
        v1 = arena[:, 6144:8192].rearrange("p (t c) -> p t c", t=TT)
        prob = arena[:, 0:1536].rearrange("p (s c k) -> p s c k", s=2, c=2)
        attnt = scratch[:, 0:768].rearrange("p (s k) -> p s k", s=2)
        attn = scratch[:, 768:1536].rearrange("p (s k) -> p s k", s=2)
        o1 = xn
        qrt = arena[:, 0:1024].rearrange("p (h c) -> p h c", h=RET_HEADS)
        krt = arena[:, 1024:2048].rearrange("p (h c) -> p h c", h=RET_HEADS)
        vr = arena[:, 2048:4096].rearrange("p (t c) -> p t c", t=TT)
        sig_r = arena[:, 0:2048].rearrange("p (t c) -> p t c", t=TT)
        sig_s = arena[:, 2048:4096].rearrange("p (t c) -> p t c", t=TT)
        ret = arena[:, 4096:6144].rearrange("p (t c) -> p t c", t=TT)
        qst = arena[:, 6144:7168].rearrange("p (h c) -> p h c", h=4)
        kvt = arena[:, 7168:7680].rearrange("p (a c) -> p a c", a=2)
        kst = arena[:, 7680:8192].rearrange("p (g c) -> p g c", g=2)
        vs = arena[:, 8192:8448].rearrange("p (t c) -> p t c", t=TT)
        scored = scratch[:, 0:1536].rearrange("p (h c) -> p h c", h=RET_HEADS)
        win = scratch[:, 0:768].rearrange("p (s k) -> p s k", s=2)
        wint = scratch[:, 768:1536].rearrange("p (s k) -> p s k", s=2)

        x_loaded = [sem(f"x_loaded{t}") for t in range(TT)]
        raw_loaded = [sem(f"raw_loaded{s}") for s in range(RING)]
        gain_loaded = [sem(f"gain_loaded{s}") for s in range(GAINS)]
        (high_made, low_made, tile_used, acth_made, actl_made, gain_used, const_loaded, ident_loaded, ws_loaded,
         p_loaded, vec_loaded, consts_set, ssq_made, eps_added, rstd_made, h_made, xn_made, xt_made,
         relu_made, squared_made, hidh_made, hidl_made, acc_done, bank_done, dve_chain, pt_made, proj_made, gate_in, gate_out,
         e_made, wst_psum, wst_made, v_gelu, v_var, v_dev, v_normed, u_gelu, st_psum, y_made,
         q_copied, k_copied, v_copied, trig_in, trig_out, lam_in, lam_out, q_roped, k_roped, qt_psum, kt_psum,
         qt_made, kt_made, score_psum, score_max, prob_made, attn_made, attnt_psum, attnt_made,
         o_psum, o_copied, o_var, o_dev, o_normed, o_trans, qrt_made, vr_made, rs_psum, rs_made, ro_psum,
         ro_var, ro_dev, ret_normed, silu_made, ret_made, ret_trans, qs_made, kv_made, ks_moved, vs_psum,
         vs_made, win_psum, win_in, win_exp, win_made, wint_psum, wint_made, wo_psum, sigr_copied, sigs_copied, gates_made,
         merged_made, merged_trans, stored) = [sem(n) for n in """
         high_made low_made tile_used acth_made actl_made gain_used const_loaded ident_loaded ws_loaded
         p_loaded vec_loaded consts_set ssq_made eps_added rstd_made h_made xn_made xt_made
         relu_made squared_made hidh_made hidl_made acc_done bank_done dve_chain pt_made proj_made gate_in gate_out
         e_made wst_psum wst_made v_gelu v_var v_dev v_normed u_gelu st_psum y_made
         q_copied k_copied v_copied trig_in trig_out lam_in lam_out q_roped k_roped qt_psum kt_psum
         qt_made kt_made score_psum score_max prob_made attn_made attnt_psum attnt_made
         o_psum o_copied o_var o_dev o_normed o_trans qrt_made vr_made rs_psum rs_made ro_psum
         ro_var ro_dev ret_normed silu_made ret_made ret_trans qs_made kv_made ks_moved vs_psum
         vs_made win_psum win_in win_exp win_made wint_psum wint_made wo_psum sigr_copied sigs_copied gates_made
         merged_made merged_trans stored""".split()]

        block = ctx.enter_context(nc.Block())


        def columns(w, c0, n=D):
            rows = w.shape[0] // 256
            return [w[j * 256:(j + 1) * 256, c0:c0 + n].rearrange("(k p) c -> p k c", p=P) for j in range(rows)]

        def rows_out(w, c0, n):
            return [w[:, c:c + 256].rearrange("(k p) c -> p k c", p=P) for c in range(c0, c0 + n, 256)]

        def split_high(act, T, lap=0):
            act.wait_ge(raw_loaded[T % RING], 16 * (T // RING + 1) + 16 * lap)
            if T >= RING:
                act.wait_ge(tile_used, T - RING + 1 + 4 * lap)
            act.copy(high[:, T % RING, :], raw[:, T % RING, :]).then_inc(high_made, 1)

        def split_low(dve, T, lap=0):
            dve.wait_ge(high_made, T + 1 + 4 * lap)
            dve.tensor_tensor(low[:, T % RING, :], raw[:, T % RING, :], high[:, T % RING, :].bitcast(F32),
                              ALU.subtract).then_inc(low_made, 1)

        @block.sync
        def _(sp):
            def load(T, src, lap=0):
                if T >= RING:
                    sp.wait_ge(low_made, T - RING + 1 + 4 * lap)
                k = src.shape[1]
                sp.dma_start(raw[:, T % RING, :].rearrange("p (k c) -> p k c", k=k), src).then_inc(
                    raw_loaded[T % RING], 16)

            def load_all(T, tiles):
                for n, src in enumerate(tiles):
                    load(T + n, src)

            def load_ffn(T, up, down):
                up_v = up.rearrange("(k p) (c q) -> c p k q", p=P, q=256)
                down_v = down.rearrange("(c k p) q -> c p k q", p=P, k=2)
                load(T, up_v[0])
                load(T + 1, up_v[1])
                load(T + 2, down_v[0])

                def dyn(v, n):
                    return v[bass.ds(n, 1)].rearrange("o p k q -> (o p) k q")

                with sp.Fori(0, FFN_CHUNKS - 1) as lap:
                    load(T + 3, dyn(up_v, lap * 2 + 2), lap)
                    load(T + 4, dyn(down_v, lap * 2 + 1), lap)
                    load(T + 5, dyn(up_v, lap * 2 + 3), lap)
                    load(T + 6, dyn(down_v, lap * 2 + 2), lap)
                load(T + 31, down_v[15])

            w_in, w_qkv, w_in2 = a["a_w_in"][0], a["b_w_qkv"][0], a["w_in_2"][0]
            x_v = a["x"][0].rearrange("(t p) c -> t p c", p=P)
            sp.dma_start(h[:, 0, :], x_v[0]).then_inc(x_loaded[0], 16)
            sp.dma_start(ident, a["consts"][:, K_ID:K_ID + P]).then_inc(ident_loaded, 16)
            load(0, columns(w_in, D)[0])
            sp.dma_start(h[:, 1, :], x_v[1]).then_inc(x_loaded[1], 16)
            load_all(1, columns(w_in, D)[1:])
            load_all(T_U0, rows_out(w_in, 0, D))
            load_all(T_OUT0, columns(a["a_w_out"][0], 0))
            load_all(T_PROJ0, columns(a["ple_w_proj"][0], 0))
            load_ffn(T_FFN0, a["f_w_up"][0], a["f_w_down"][0])
            load_all(T_GATE0, columns(a["ple_w_gate"][0], 0))
            load_all(T_Q, columns(w_qkv, 0))
            load_all(T_K, columns(w_qkv, D))
            load_all(T_V, [w_qkv[r:r + 512, c:c + BANK].rearrange("(k p) c -> p k c", p=P)
                           for c in (2 * D, 2 * D + BANK) for r in (0, 512)])
            load_all(T_WO, columns(a["b_w_o"][0], 0))
            load_all(T_PROJ1, columns(a["ple_w_proj"][1], 0))
            load_ffn(T_FFN1, a["f_w_up"][1], a["f_w_down"][1])
            load_all(T_GATE1, columns(a["ple_w_gate"][1], 0))
            load_all(T_VR, columns(w_in2, 1024))
            load_all(T_GR, columns(w_in2, 2048))
            load_all(T_QR, rows_out(w_in2, 0, 512))
            load_all(T_KR, rows_out(w_in2, 512, 512))
            load_all(T_QS, rows_out(w_in2, 3072, 512))
            load_all(T_KVS, rows_out(w_in2, 3584, 256))
            load_all(T_GATER, columns(w_in2, 3840))
            load_all(T_GATES, columns(w_in2, 4864))
            load_all(T_RET, columns(a["w_ret_out_2"][0], 0))
            load_all(T_SWA, columns(a["w_swa_out_2"][0], 0))
            load_all(T_OUT2, columns(a["w_out_2"][0], 0))
            load_ffn(T_FFN2, a["w_up_2"][0], a["w_down_2"][0])
            out_v = out[0].rearrange("(t p) c -> t p c", p=P)
            for t in range(TT):
                for b in range(2):
                    cols = slice(b * BANK, b * BANK + BANK)
                    sp.wait_ge(h_made, h_halves(8, t, b))
                    sp.dma_start(out_v[t, :, cols], h[:, t, cols]).then_inc(stored, 16)
            sp.wait_ge(stored, 16 * 2 * TT)

        @block.gpsimd
        def _(pool):
            gains = [a["g_mix_pre"][0:1], a["a_ln_g"][0:1], a["a_ln_b"][0:1], a["g_mix_post"][0:1],
                     a["g_ffn_pre"][0:1], a["g_ffn_post"][0:1], a["g_ple_pre"][0:1], a["ple_b_gate"][0:1],
                     a["g_ple_post"][0:1], a["g_mix_pre"][1:2], a["g_mix_post"][1:2], a["g_ffn_pre"][1:2],
                     a["g_ffn_post"][1:2], a["g_ple_pre"][1:2], a["ple_b_gate"][1:2], a["g_ple_post"][1:2],
                     a["pre_mix_norm_2"], a["post_mix_norm_2"], a["pre_mlp_norm_2"], a["post_mlp_norm_2"]]

            freed = {G_LNG: (gain_used, 2), G_LNB: (v_normed, 2), G_BG0: (gate_in, 2), G_BG1: (gate_in, 4)}
            for j, g in enumerate(GAIN_PRE):
                freed[g] = (xn_made, 4 * j + 4)
            for j, g in enumerate(GAIN_POST):
                freed[g] = (h_made, 4 * j + 4)

            def load_gain(n):
                if n >= GAINS:
                    pool.wait_ge(*freed[n - GAINS])
                pool.dma_start(gain[:, n % GAINS, :], gains[n].broadcast_to([P, D])).then_inc(
                    gain_loaded[n % GAINS], 16)

            def load_p(layer):
                pool.dma_start(ptok[:, :, :], a["p"][layer, 0].rearrange("(t p) c -> p t c", p=P)).then_inc(
                    p_loaded, 16)

            added = [0]

            with_eps = ms[:, 1, :]

            def to_dev(dst, with_eps, src, eps, scale=1.0):
                added[0] += 1
                pool.tensor_scalar(with_eps, src, scale, eps, ALU.mult, ALU.add).then_inc(eps_added, 1)
                pool.wait_ge(eps_added, added[0])
                return pool.tensor_tensor(dst, with_eps, minus_half[:, 0:src.shape[1]], ALU.pow)

            def rms(j, t):
                for kind in (("post",) if j >= 1 else ()) + (("pre",) if j <= 7 else ()):
                    n = RMS[kind, j, t]
                    pool.wait_ge(ssq_made, 2 * n + 2)
                    added[0] += 1
                    pool.tensor_scalar(with_eps[:, n:n + 1], ms[:, 0, n:n + 1], ms[:, 1, n:n + 1], RMS_EPS,
                                       ALU.add, ALU.add).then_inc(eps_added, 1)
                    pool.wait_ge(eps_added, added[0])
                    pool.tensor_tensor(rstd[:, n:n + 1], with_eps[:, n:n + 1], minus_half[:, 0:1], ALU.pow).then_inc(
                        rstd_made, 1)

            load_gain(0)
            load_p(0)
            pool.memset(minus_half[:, :], -0.5).then_inc(consts_set, 1)
            pool.wait_ge(consts_set, 1)
            for t in range(TT):
                rms(0, t)
            pool.dma_start(ws_raw, a["a_w_s"][0].rearrange("g t s -> t g s")).then_inc(ws_loaded, 16)
            pool.dma_start(bs, a["a_b_s"].rearrange("a g t -> a (g t)").broadcast_to([P, D])
                           .rearrange("p (g c) -> p g c", g=8)).then_inc(ws_loaded, 16)
            pool.dma_start(cst[:, P:], a["consts"][:, P:]).then_inc(const_loaded, 16)
            for n, name in enumerate(("b_lam_q1", "b_lam_q2", "b_lam_k1", "b_lam_k2")):
                pool.dma_start(vecs[:, 64 * n:64 * n + 64], a[name].broadcast_to([P, 64])).then_inc(vec_loaded, 16)
            pool.dma_start(vecs[:, 256:384], a["b_subln_g"].broadcast_to([P, P])).then_inc(vec_loaded, 16)
            pool.dma_start(vecs[:, 384:392], a["sinks_2"].broadcast_to([P, 8])).then_inc(vec_loaded, 16)
            pool.dma_start(pos_i[:, :], a["positions"].rearrange("a (t p) -> p (a t)", p=P),
                           allow_slow_non_contiguous=True).then_inc(vec_loaded, 16)
            load_gain(1)
            load_gain(2)
            pool.wait_ge(pt_made, 1)
            load_p(1)
            for t in range(TT):
                pool.wait_ge(v_var, t + 1)
                to_dev(dev[:, t:t + 1], mv_eps[:, t:t + 1], mv[:, t, 1:2], LN_EPS).then_inc(v_dev, 1)
            load_gain(3)
            load_gain(4)
            load_gain(5)
            for t in range(TT):
                rms(1, t)
            load_gain(6)
            load_gain(7)
            for t in range(TT):
                rms(2, t)
            load_gain(8)
            load_gain(9)
            for t in range(TT):
                rms(3, t)
            load_gain(10)
            load_gain(11)
            load_gain(12)
            for hd in range(HEADS):
                pool.wait_ge(o_var, hd + 1)
                to_dev(o_ms[:, 2, hd, :], o_ms[:, 1, hd, :], o_ms[:, 0, hd, :], SUBLN_EPS, 1.0 / P).then_inc(o_dev, 1)
            for t in range(TT):
                rms(4, t)
            load_gain(13)
            load_gain(14)
            for t in range(TT):
                rms(5, t)
            load_gain(15)
            load_gain(16)
            for t in range(TT):
                rms(6, t)
            load_gain(17)
            load_gain(18)
            load_gain(19)
            for hd in range(RET_HEADS):
                c = 2 + 2 * hd
                pool.wait_ge(ro_var, hd + 1)
                to_dev(dev[:, c:c + 2], mv_eps[:, c:c + 2], mv[:, c:c + 2, 1], RET_EPS).then_inc(ro_dev, 1)
            pool.wait_ge(kv_made, 1)
            for g in range(2):
                for half in range(2):
                    pool.dma_start(kst[64 * half:64 * half + 64, g, :],
                                   kvt[64 * g:64 * g + 64, 0, :]).then_inc(ks_moved, 16)
            for t in range(TT):
                rms(7, t)
            for t in range(TT):
                rms(8, t)

        @block.scalar
        def _(act):
            split = [0]

            def splits_through(T):
                while split[0] <= min(T, T_END - 1):
                    split_high(act, split[0])
                    split[0] += 1

            def convert(step, src, dst, made, value):
                act.wait_ge(made, value)
                act.copy(dst, src).then_inc(acth_made, 1)

            def convert_transposed(first, acc, made, value):
                for t in range(TT):
                    for b in range(2):
                        convert(first + 2 * t + b, bank4(acc + 2 * t + b), act_part(acth, t, b),
                                made, value + 2 * t + b + 1)

            def wait_product(n, T, t):
                if t == 0:
                    act.wait_ge(acc_done, n + 1)
                else:
                    act.wait_ge(tile_used, T + 1)

            def square_sum(kind, j, t, b, src):
                n = RMS[kind, j, t]
                if n >= 2:
                    act.wait_ge(ssq_made, 2 * n + b - 3)
                act.activation(half_of(junk, n % 2, b), src, ACT.Square, scale=1 / 32,
                               accum_out=ms[:, b, n:n + 1]).then_inc(ssq_made, 1)

            def squares_post(j, t, ready=None):
                in_psum = ready is not None
                for b in range(2):
                    if in_psum and b == 0:
                        act.wait_ge(bank_done, 2 * OUTPUTS[j] + t + 1)
                    elif in_psum:
                        ready(t)
                    square_sum("post", j, t, b, ps[:, Y + 2 * t + b, :] if in_psum else half_of(xn, t, b))

            def squares_pre(j, t):
                for b in range(2):
                    if j >= 1:
                        act.wait_ge(h_made, h_halves(j, t, b))
                    square_sum("pre", j, t, b, half_of(h, t, b))

            def boundary(j, T, ready=None, beside=True, between=None):
                for t in range(TT):
                    if j >= 1:
                        squares_post(j, t, ready)
                    else:
                        act.wait_ge(x_loaded[t], 16)
                    if j >= 1:
                        splits_through(T + 2 * t)
                    squares_pre(j, t)
                    if j == 0:
                        splits_through(T + 3 * t)
                    else:
                        splits_through(T + 1 + t + (t and beside))
                    if t and between:
                        between()
                    for b in range(2):
                        convert(C_PRE[j] + 2 * t + b, bank4(Y + 2 * t + b), act_part(acth, t, b),
                                xt_made, 4 * j + 2 * t + b + 1)
                splits_through(T + 3)

            def product_ready(n, T):
                return lambda t: wait_product(n, T, t)

            def hidden(T, half, n, lap=0):
                act.wait_ge(tile_used, T + 1 + 4 * lap)
                if not isinstance(n, int) or n >= 2:
                    act.wait_ge(hidl_made, n - 1)
                act.activation(relu[:, half, :], ps[:, X + half, :], ACT.Relu).then_inc(relu_made, 1)
                act.wait_ge(relu_made, n + 1)
                act.activation(hidh[:, half, :], relu[:, half, :], ACT.Square).then_inc(hidh_made, 1)

            def projection(product, T):
                def copies():
                    for t in range(TT):
                        wait_product(product, T, t)
                        act.copy(pair(proj, t), acc_pair(X, t)).then_inc(proj_made, 1)
                return copies

            def ffn(f):
                T, n = FFN_TILES[f], 16 * f
                splits_through(T + 3)
                hidden(T, 0, n)
                splits_through(T + 4)
                hidden(T + 1, 1, n + 1)
                splits_through(T + 5)

                def chunk(lap, last=False):
                    split_high(act, T + 6, lap)
                    hidden(T + 3, 0, n + 2 + 2 * lap, lap)
                    split_high(act, T + 7, lap)
                    if not last:
                        split_high(act, T + 8, lap)
                    hidden(T + 5, 1, n + 3 + 2 * lap, lap)
                    if not last:
                        split_high(act, T + 9, lap)

                last = f == 2
                with act.Fori(0, FFN_CHUNKS - 1 - last) as lap:
                    chunk(lap)
                if last:
                    chunk(FFN_CHUNKS - 2, True)
                split[0] = T + 34

            def sigmoids(layer, t):
                act.wait_ge(gate_in, 2 * layer + t + 1)
                act.activation(xn[:, t, :], xn[:, t, :], ACT.Sigmoid).then_inc(gate_out, 1)

            def gated_boundary(j, T, layer):
                sigmoids(layer, 0)
                for t in range(TT):
                    act.wait_ge(e_made, 2 * layer + t + 1)
                    squares_post(j, t)
                    splits_through(T + 3 * t)
                    squares_pre(j, t)
                    splits_through(T + 2 + t)
                    for b in range(2):
                        convert(C_PRE[j] + 2 * t + b, bank4(Y + 2 * t + b), act_part(acth, t, b),
                                xt_made, 4 * j + 2 * t + b + 1)
                    if t == 0:
                        sigmoids(layer, 1)
                        splits_through(T + 3)

            boundary(0, T_V0)
            convert(C_P[0], ps[:, Y, :], flat(ph), pt_made, 1)

            for t in range(TT):
                wait_product(A_V0, T_V0 + 3, t)
                act.activation(pair(v0, t), acc_pair(X, t), ACT.Gelu_apprx_tanh).then_inc(v_gelu, 1)
                splits_through(T_U0 + (2, 3)[t])
            for j in range(4):
                act.wait_ge(tile_used, T_U0 + j + 1)
                act.activation(ut[:, j, :], ps[:, Y + j, :], ACT.Gelu_apprx_tanh).then_inc(u_gelu, 1)
                if j == 3:
                    for b in range(4):
                        convert(C_Y0 + b, xn_bank(b), flat(acth[:, 2 * b:2 * b + 2, :]), y_made, b + 1)
                splits_through(T_U0 + j + LEAD + 1)
            act.wait_ge(trig_in, 1)
            act.activation(trig[:, :, :, :], trig_arg[:, :, :, :], ACT.Sin).then_inc(trig_out, 1)
            act.wait_ge(lam_in, 1)
            act.activation(lam[:, 130:132], lam[:, 128:130], ACT.Exp).then_inc(lam_out, 1)
            boundary(1, T_PROJ0, product_ready(A_OUT0, T_OUT0 + 3), beside=False,
                     between=projection(A_PROJ0, T_PROJ0))
            ffn(0)
            boundary(2, T_GATE0, product_ready(A_FFN0, T_FFN0 + 31))
            convert(C_P[1], ps[:, X + 2, :], flat(ph), pt_made, 2)
            splits_through(T_GATE0 + 3)
            gated_boundary(3, T_Q, 0)

            splits_through(T_Q + 3)
            for t in range(TT):
                wait_product(A_Q, T_Q + 3, t)
                act.copy(pair(qtok, t), acc_pair(Y, t)).then_inc(q_copied, 1)
                splits_through(T_K + (2, 3)[t])
            for t in range(TT):
                wait_product(A_K, T_K + 3, t)
                act.copy(pair(xn, t), acc_pair(X, t)).then_inc(k_copied, 1)
                splits_through(T_V + (2, 3)[t])
            for b in range(4):
                act.wait_ge(kt_psum, b + 1)
                act.copy(flat(kt_[:, 2 * b:2 * b + 2, :]), ps[:, X + b, :]).then_inc(kt_made, 1)

            def copy_v(n):
                act.wait_ge(tile_used, T_V + 2 * n + 2)
                act.copy(v1[:, :, n * BANK:n * BANK + BANK], ps[:, Y:Y + 2, :]).then_inc(v_copied, 1)

            copy_v(0)

            def exponentials(i):
                s = i % 2
                act.wait_ge(score_max, i + 1)
                if i >= 2:
                    act.wait_ge(attn_made, i - 1)
                else:
                    act.wait_ge(qt_psum, 4)
                for c in range(2):
                    for blk, (lo, hi) in enumerate(((0, 128), (128, 384))):
                        k = 2 * blk + c
                        ins = act.activation(prob[:, s, c, lo:hi], ps[:, X + 2 * s + c, lo:hi], ACT.Exp,
                                             bias=soft[:, s, 4 + k:5 + k], scale=0.125,
                                             accum_out=soft[:, s, 8 + k:9 + k])
                ins.then_inc(prob_made, 1)

            def copy_attnt(i):
                act.wait_ge(attnt_psum, i + 1)
                if i >= 2:
                    act.wait_ge(o_psum, i - 1)
                act.copy(attnt[:, i % 2, :], ps[:, Y + 2 + i % 2, 0:384]).then_inc(attnt_made, 1)

            def copy_o(i):
                act.wait_ge(o_psum, i + 1)
                for t in range(TT):
                    last = act.activation(junk[:, t, P * i:P * i + P], ps[:, Y + 2 + i % 2, P * t:P * t + P],
                                          ACT.Square, accum_out=o_ms[:, 0, i, t:t + 1])
                last.then_inc(o_var, 1)
                act.copy(o1[:, :, P * i:P * i + P],
                         ps[:, Y + 2 + i % 2, 0:256].rearrange("p (t c) -> p t c", t=2)).then_inc(o_copied, 1)

            def convert_o(half):
                for t in range(TT):
                    n = 2 * half + t
                    convert(C_O1 + n, bank4((X if half else Y) + t), act_part(acth, t, half), o_trans, n + 1)

            for i in range(HEADS + 2):
                if i < HEADS:
                    exponentials(i)
                if i == 2:
                    copy_v(1)
                if 1 <= i <= HEADS:
                    copy_attnt(i - 1)
                if i == HEADS + 1:
                    convert_o(0)
                if i >= 2:
                    copy_o(i - 2)
                splits_through(T_WO + (0, 1, 1, 2, 3)[min(i, 4)])
            convert_o(1)
            boundary(4, T_PROJ1, product_ready(A_WO, T_WO + 3), beside=False,
                     between=projection(A_PROJ1, T_PROJ1))
            ffn(1)
            boundary(5, T_GATE1, product_ready(A_FFN1, T_FFN1 + 31))
            splits_through(T_GATE1 + 3)
            gated_boundary(6, T_VR, 1)

            splits_through(T_VR + 3)
            for t in range(TT):
                wait_product(A_VR, T_VR + 3, t)
                act.copy(pair(vr, t), acc_pair(Y, t)).then_inc(vr_made, 1)
                splits_through(T_GR + (2, 3)[t])
            for t in range(TT):
                wait_product(A_GR, T_GR + 3, t)
                act.activation(pair(xn, t), acc_pair(X, t), ACT.Silu).then_inc(silu_made, 1)
                splits_through(T_QR + (2, 3)[t])
            for j in range(4):
                act.wait_ge(tile_used, T_QR + j + 1)
                dst = qrt if j < 2 else krt
                act.copy(flat(dst[:, 2 * (j % 2):2 * (j % 2) + 2, :]), ps[:, Y + j, :]).then_inc(qrt_made, 1)
                splits_through(T_QR + j + 1 + LEAD)
            for j in range(2):
                act.wait_ge(tile_used, T_QS + j + 1)
                act.copy(flat(qst[:, 2 * j:2 * j + 2, :]), ps[:, Y + j, :]).then_inc(qs_made, 1)
                splits_through(T_QS + j + 1 + LEAD)
            act.wait_ge(tile_used, T_KVS + 1)
            act.copy(flat(kvt), ps[:, Y + 2, :]).then_inc(kv_made, 1)

            def window_exp(i):
                s = i % 2
                act.wait_ge(win_in, i + 1)
                for blk, (lo, hi) in enumerate(((0, 128), (128, 384))):
                    act.activation(win[:, s, lo:hi], win[:, s, lo:hi], ACT.Exp, bias=soft[:, s, 2 + blk:3 + blk],
                                   scale=0.125, accum_out=soft[:, s, 4 + blk:5 + blk])
                act.activation(soft[:, s, 6:8], soft[:, s, 2:4], ACT.Exp,
                               bias=vecs[:, 384 + i:385 + i]).then_inc(win_exp, 1)

            def copy_wint(i):
                act.wait_ge(wint_psum, i + 1)
                if i >= 2:
                    act.wait_ge(wo_psum, i - 1)
                act.copy(wint[:, i % 2, :], ps[:, Y + 2, 0:384]).then_inc(wint_made, 1)

            def copy_gate(product, T, t, dst, made):
                wait_product(product, T, t)
                act.copy(pair(dst, t), acc_pair(X, t)).then_inc(made, 1)

            for i in range(SWA_HEADS + 2):
                if i == 3:
                    copy_gate(A_GATER, T_GATER + 3, 0, sig_r, sigr_copied)
                    splits_through(T_GATER + 2 + LEAD)
                if i == 7:
                    copy_gate(A_GATES, T_GATES + 3, 0, sig_s, sigs_copied)
                if i == 0:
                    act.wait_ge(vs_psum, 1)
                    act.copy(flat(vs), ps[:, Y + 3, 0:256]).then_inc(vs_made, 1)
                if i == 3:
                    copy_gate(A_GATER, T_GATER + 3, 1, sig_r, sigr_copied)
                if i == 7:
                    copy_gate(A_GATES, T_GATES + 3, 1, sig_s, sigs_copied)
                if i < SWA_HEADS:
                    window_exp(i)
                if i == 8:
                    convert_transposed(C_RET, X, ret_trans, 0)
                if i >= 2:
                    copy_wint(i - 2)
                if i == 6:
                    convert(C_SWA[0], ps[:, Y + 3, :], hidh[:, 0, :], wo_psum, 4)
                if i < 5 and i != 2:
                    splits_through(T_GATER + i + LEAD)
                if i in (6, 8):
                    splits_through(T_RET + i - 6)
            splits_through(T_RET + 3)
            convert(C_SWA[1], ps[:, Y + 3, :], hidh[:, 1, :], wo_psum, 8)
            for t in range(TT):
                for gate, copied in ((sig_r, sigr_copied), (sig_s, sigs_copied)):
                    act.wait_ge(copied, t + 1)
                    act.activation(gate[:, t, :], gate[:, t, :], ACT.Sigmoid).then_inc(gates_made, 1)
                splits_through(T_SWA + 1 + t)
            for t in range(TT):
                for b in range(2):
                    convert(C_MERGED + 2 * t + b, bank4(X + 2 * t + b), act_part(acth, t, b), merged_trans,
                            2 * t + b + 1)
                splits_through(T_OUT2 + 3)
            boundary(7, T_FFN2, product_ready(A_OUT2, T_OUT2 + 3), beside=False)
            ffn(2)
            for t in range(TT):
                squares_post(8, t, product_ready(A_FFN2, T_FFN2 + 31))

        @block.vector
        def _(dve):
            split = [0]
            chain = [0]

            def splits_through(T):
                while split[0] <= min(T, T_END - 1):
                    split_low(dve, split[0])
                    split[0] += 1

            def link(ins):
                chain[0] += 1
                ins.then_inc(dve_chain, 1)
                dve.wait_ge(dve_chain, chain[0])

            def gained(n):
                dve.wait_ge(gain_loaded[n % GAINS], 16 * (n // GAINS + 1))

            def convert(step, src, high_part, low_part):
                dve.wait_ge(acth_made, step + 1)
                dve.tensor_tensor(low_part, src, high_part.bitcast(F32), ALU.subtract).then_inc(actl_made, 1)

            def convert_transposed(first, acc):
                for t in range(TT):
                    for b in range(2):
                        convert(first + 2 * t + b, bank4(acc + 2 * t + b), act_part(acth, t, b),
                                act_part(actl, t, b))

            def add_to_h(j, t, in_psum=True, through=0):
                g = GAIN_POST[j - 1]
                gained(g)
                n = RMS["post", j, t]
                for b in range(2):
                    src = ps[:, Y + 2 * t + b, :] if in_psum else half_of(xn, t, b)
                    chain[0] += 1
                    if t:
                        dve.wait_ge(h_made, h_halves(j, 0, b))
                    if in_psum:
                        dve.wait_ge(ssq_made, 2 * n + b + 1)
                    dve.tensor_tensor(weighed[:, b, :], src, half_of(gain, g % GAINS, b), ALU.mult).then_inc(
                        dve_chain, 1)
                weighed_at = chain[0]
                splits_through(through)
                dve.wait_ge(rstd_made, n + 1)
                for b in range(2):
                    dve.wait_ge(dve_chain, weighed_at - 1 + b)
                    dve.scalar_tensor_tensor(half_of(h, t, b), weighed[:, b, :], rstd[:, n:n + 1], half_of(h, t, b),
                                             ALU.mult, ALU.add).then_inc(h_made, 1)

            def norm_h(j, t):
                g = GAIN_PRE[j]
                gained(g)
                n = RMS["pre", j, t]
                if j >= 1:
                    dve.wait_ge(h_made, h_halves(j, t, 1))
                dve.wait_ge(rstd_made, n + 1)
                for b in range(2):
                    dve.scalar_tensor_tensor(half_of(xn, t, b), half_of(h, t, b), rstd[:, n:n + 1],
                                             half_of(gain, g % GAINS, b), ALU.mult, ALU.mult).then_inc(xn_made, 1)

            def convert_tile(first, acc, t):
                for b in range(2):
                    convert(first + 2 * t + b, bank4(acc + 2 * t + b), act_part(acth, t, b), act_part(actl, t, b))

            def boundary(j, T, beside=True):
                for t in range(TT):
                    add_to_h(j, t)
                    splits_through(T + 2 * t)
                    norm_h(j, t)
                    splits_through(T + 1 + t + (t and beside))
                    convert_tile(C_PRE[j], Y, t)
                splits_through(T + 3)

            def gated_boundary(j, T, layer, product, last_tile, bias):
                gained(bias)

                def biased(t):
                    dve.wait_ge(*((tile_used, last_tile + 1) if t else (acc_done, product + 1)))
                    dve.tensor_tensor(pair(xn, t), acc_pair(Y, t), pair(gain, bias % GAINS), ALU.add).then_inc(
                        gate_in, 1)

                biased(0)
                for t in range(TT):
                    dve.wait_ge(gate_out, 2 * layer + t + 1)
                    dve.wait_ge(proj_made, 2 * layer + t + 1)
                    dve.tensor_tensor(xn[:, t, :], xn[:, t, :], proj[:, t, :], ALU.mult).then_inc(e_made, 1)
                    dve.wait_ge(e_made, 2 * layer + t + 1)
                    add_to_h(j, t, in_psum=False, through=T + 2 if t else 0)
                    splits_through(T + 3 * t)
                    norm_h(j, t)
                    if t == 0:
                        biased(1)
                    convert_tile(C_PRE[j], Y, t)
                    if t == 0:
                        splits_through(T + 1)
                splits_through(T + 3)

            def hidden(half, n):
                dve.wait_ge(relu_made, n + 1)
                if not isinstance(n, int) or n >= 1:
                    dve.wait_ge(hidl_made, n)
                dve.tensor_tensor(squared, relu[:, half, :], relu[:, half, :], ALU.mult).then_inc(squared_made, 1)
                dve.wait_ge(squared_made, n + 1)
                dve.wait_ge(hidh_made, n + 1)
                dve.tensor_tensor(hidl[:, half, :], squared, hidh[:, half, :].bitcast(F32),
                                  ALU.subtract).then_inc(hidl_made, 1)

            def ffn(f):
                T, n = FFN_TILES[f], 16 * f
                splits_through(T + 3)
                hidden(0, n)
                splits_through(T + 4)
                hidden(1, n + 1)
                splits_through(T + 5)

                def chunk(lap, last=False):
                    split_low(dve, T + 6, lap)
                    hidden(0, n + 2 + 2 * lap)
                    split_low(dve, T + 7, lap)
                    if not last:
                        split_low(dve, T + 8, lap)
                    hidden(1, n + 3 + 2 * lap)
                    if not last:
                        split_low(dve, T + 9, lap)

                last = f == 2
                with dve.Fori(0, FFN_CHUNKS - 1 - last) as lap:
                    chunk(lap)
                if last:
                    chunk(FFN_CHUNKS - 2, True)
                split[0] = T + 34

            norm_h(0, 0)
            splits_through(T_V0)
            convert_tile(C_PRE[0], Y, 0)
            norm_h(0, 1)
            splits_through(T_V0 + 2)
            convert_tile(C_PRE[0], Y, 1)
            splits_through(T_V0 + 3)
            convert(C_P[0], ps[:, Y, :], flat(ph), flat(pl))
            dve.wait_ge(const_loaded, 16)
            for b in range(2):
                dve.wait_ge(wst_psum, b + 1)
                dve.tensor_tensor(wst[:, 4 * b:4 * b + 4, :], bank4(Y + 1 + b), repeat(cst[:, K_TRIU:K_TRIU + P], 4),
                                  ALU.mult).then_inc(wst_made, 1)

            for t in range(TT):
                dve.wait_ge(v_gelu, t + 1)
                for b in range(2):
                    last = dve.bn_stats(bn[:, t, 6 * b:6 * b + 6], v0[:, t, BANK * b:BANK * b + BANK])
                link(last)
                dve.bn_aggr(mv[:, t, :], bn[:, t, :]).then_inc(v_var, 1)
                splits_through(T_U0 + 2 * t)
                gained(G_LNG)
                gained(G_LNB)
                dve.wait_ge(v_var, t + 1)
                dve.wait_ge(v_dev, t + 1)
                link(dve.tensor_scalar(v0[:, t, :], v0[:, t, :], mv[:, t, 0:1], dev[:, t:t + 1], ALU.subtract,
                                       ALU.mult))
                dve.tensor_tensor(v0[:, t, :], v0[:, t, :], gain[:, G_LNG % GAINS, :], ALU.mult).then_inc(gain_used, 1)
                dve.wait_ge(gain_used, t + 1)
                dve.tensor_tensor(v0[:, t, :], v0[:, t, :], gain[:, G_LNB % GAINS, :], ALU.add).then_inc(v_normed, 1)
                splits_through(T_U0 + (1, 3)[t])

            def mix(b):
                dve.wait_ge(st_psum, b + 1)
                sbank = ps[:, X + b, :].rearrange("p (g n c) -> p g n c", g=2, n=2)
                ybank = xn_bank(b).rearrange("p (g n c) -> p g n c", g=2, n=2)
                for g in range(2):
                    last = dve.tensor_tensor(ybank[:, g], sbank[:, g], repeat(bs[:, 2 * b + g, :], 2), ALU.add)
                link(last)
                dve.wait_ge(u_gelu, b + 1)
                dve.tensor_tensor(xn_bank(b), xn_bank(b), ut[:, b, :], ALU.mult).then_inc(y_made, 1)

            def convert_y(b):
                dve.wait_ge(y_made, b + 1)
                convert(C_Y0 + b, xn_bank(b), flat(acth[:, 2 * b:2 * b + 2, :]), flat(actl[:, 2 * b:2 * b + 2, :]))

            splits_through(T_OUT0)
            mix(0)
            mix(1)
            splits_through(T_OUT0 + 1)
            mix(2)
            convert_y(0)
            mix(3)
            for b in range(1, 4):
                convert_y(b)
            splits_through(T_OUT0 + 3)
            dve.wait_ge(wst_made, 2)
            dve.tensor_copy(ident16[:, :], ident)
            triu = cst[:, K_TRIU:K_TRIU + P]
            link(dve.tensor_tensor(triu, triu, ident, ALU.subtract))
            link(dve.tensor_scalar(causal16[:, :], triu, -1e30, None, ALU.mult))

            dve.wait_ge(vec_loaded, 7 * 16)
            link(dve.tensor_copy(pos_f[:, :], pos_i[:, :]))
            for t in range(TT):
                last = dve.tensor_scalar(trig_arg[:, 0, t, :], cst[:, K_FREQ:K_FREQ + 8], pos_f[:, t:t + 1], None,
                                         ALU.mult)
            link(last)
            link(dve.tensor_scalar(trig_n[:, :, :], trig_arg[:, 0], 0.5 / math.pi, ROUND_MAGIC, ALU.mult, ALU.add))
            link(dve.tensor_scalar(trig_n[:, :, :], trig_n[:, :, :], ROUND_MAGIC, None, ALU.subtract))
            for part in TWO_PI_PARTS:
                link(dve.scalar_tensor_tensor(trig_arg[:, 0], trig_n[:, :, :], -part, trig_arg[:, 0],
                                              ALU.mult, ALU.add))
            link(dve.tensor_scalar(trig_arg[:, 1], trig_arg[:, 0], 0.5 * math.pi, None, ALU.add))
            link(dve.tensor_scalar(trig_n[:, :, :], trig_arg[:, 1], math.pi, -2 * math.pi, ALU.is_gt, ALU.mult))
            link(dve.tensor_tensor(trig_arg[:, 1], trig_arg[:, 1], trig_n[:, :, :], ALU.add))
            dve.tensor_scalar(trig_arg[:, :, :, :], trig_arg[:, :, :, :], 3.1415925, -3.1415925, ALU.min,
                              ALU.max).then_inc(trig_in, 1)
            link(dve.tensor_tensor(lam[:, 0:128], vecs[:, 0:128], vecs[:, 128:256], ALU.mult))
            dve.tensor_reduce(lam[:, 128:130], lam[:, 0:128].rearrange("p (n c) -> p n c", n=2), AX_X,
                              ALU.add).then_inc(lam_in, 1)
            link(dve.tensor_scalar(vecs[:, 256:384], vecs[:, 256:384], 1.0 - LAMBDA_INIT, None, ALU.mult))
            link(dve.tensor_scalar(sink8[:, :], vecs[:, 384:392], 8.0, None, ALU.mult))
            dve.wait_ge(lam_out, 1)
            link(dve.tensor_tensor(lam[:, 132:133], lam[:, 131:132], lam[:, 130:131], ALU.subtract))
            link(dve.tensor_scalar(lam[:, 133:134], lam[:, 132:133], -LAMBDA_INIT, None, ALU.add))
            boundary(1, T_PROJ0, beside=False)
            ffn(0)
            boundary(2, T_GATE0)
            convert(C_P[1], ps[:, X + 2, :], flat(ph), flat(pl))
            splits_through(T_GATE0 + 3)
            gated_boundary(3, T_Q, 0, A_GATE0, T_GATE0 + 3, G_BG0)

            def rotate(tok, t, made, before=None):
                if before:
                    dve.wait_ge(*before)
                x = tok[:, t, :].rearrange("p (n c) -> p n c", c=64)
                cos, sin = repeat(trig[:, 1, t, :], 16), repeat(trig[:, 0, t, :], 16)
                tmp = scratch[:, 0:512].rearrange("p (a n c) -> p a n c", a=4, c=8)
                x1, x2 = x[:, :, 0:8], x[:, :, 8:16]
                dve.tensor_tensor(tmp[:, 0], x1, cos, ALU.mult)
                dve.tensor_tensor(tmp[:, 1], x2, sin, ALU.mult)
                dve.tensor_tensor(tmp[:, 2], x2, cos, ALU.mult)
                link(dve.tensor_tensor(tmp[:, 3], x1, sin, ALU.mult))
                dve.tensor_tensor(x1, tmp[:, 0], tmp[:, 1], ALU.subtract)
                dve.tensor_tensor(x2, tmp[:, 2], tmp[:, 3], ALU.add).then_inc(made, 1)

            dve.wait_ge(trig_out, 1)
            splits_through(T_Q + 3)
            for t in range(TT):
                dve.wait_ge(q_copied, t + 1)
                rotate(qtok, t, q_roped, (q_roped, 1) if t else None)
                splits_through(T_K + (2, 3)[t])
            for t in range(TT):
                dve.wait_ge(k_copied, t + 1)
                rotate(xn, t, k_roped, (k_roped, 1) if t else (q_roped, 2))
                if t == 0:
                    for b in range(4):
                        dve.wait_ge(qt_psum, b + 1)
                        dve.tensor_copy(flat(qt[:, 2 * b:2 * b + 2, :]), ps[:, Y + b, :]).then_inc(qt_made, 1)
                splits_through(T_V + (2, 3)[t])

            def maxima(i):
                s = i % 2
                dve.wait_ge(score_psum, i + 1)
                sc = ps[:, X + 2 * s:X + 2 * s + 2, :]
                dve.tensor_reduce(soft[:, s, 0:2], sc[:, :, 0:128], AX_X, ALU.max)
                link(dve.tensor_reduce(soft[:, s, 2:4], sc[:, :, 128:384], AX_X, ALU.max))
                dve.tensor_scalar(soft[:, s, 4:8], soft[:, s, 0:4], -0.125, None, ALU.mult).then_inc(score_max, 1)

            def combine(i):
                s = i % 2
                dve.wait_ge(prob_made, i + 1)
                if i >= 2:
                    dve.wait_ge(attnt_psum, i - 1)
                link(dve.reciprocal(soft[:, s, 12:16], soft[:, s, 8:12]))
                link(dve.tensor_scalar(soft[:, s, 13:16:2], soft[:, s, 13:16:2], lam[:, 133:134], None, ALU.mult))
                for blk, (lo, hi) in enumerate(((0, 128), (128, 384))):
                    last = dve.tensor_scalar(prob[:, s, 1, lo:hi], prob[:, s, 1, lo:hi],
                                             soft[:, s, 13 + 2 * blk:14 + 2 * blk], None, ALU.mult)
                link(last)
                for blk, (lo, hi) in enumerate(((0, 128), (128, 384))):
                    last = dve.scalar_tensor_tensor(attn[:, s, lo:hi], prob[:, s, 0, lo:hi],
                                                    soft[:, s, 12 + 2 * blk:13 + 2 * blk], prob[:, s, 1, lo:hi],
                                                    ALU.mult, ALU.add)
                last.then_inc(attn_made, 1)

            def norm_o(i):
                dve.wait_ge(o_dev, i + 1)
                dve.wait_ge(o_copied, i + 1)
                for t in range(TT):
                    o_head = o1[:, t, P * i:P * i + P]
                    last = dve.scalar_tensor_tensor(o_head, o_head, o_ms[:, 2, i, t:t + 1], vecs[:, 256:384],
                                                    ALU.mult, ALU.mult)
                last.then_inc(o_normed, 1)

            def convert_o(half):
                for t in range(TT):
                    convert(C_O1 + 2 * half + t, bank4((X if half else Y) + t), act_part(acth, t, half),
                            act_part(actl, t, half))

            maxima(0)
            for i in range(HEADS):
                if i + 1 < HEADS:
                    maxima(i + 1)
                combine(i)
                if i >= 3:
                    norm_o(i - 3)
                splits_through(T_WO + (0, 1, 1, 2, 3)[min(i, 4)])
            norm_o(5)
            norm_o(6)
            convert_o(0)
            norm_o(7)
            convert_o(1)
            boundary(4, T_PROJ1, beside=False)
            ffn(1)
            boundary(5, T_GATE1)
            splits_through(T_GATE1 + 3)
            gated_boundary(6, T_VR, 1, A_GATE1, T_GATE1 + 3, G_BG1)

            splits_through(T_KR + 1 + LEAD)
            for hd in range(RET_HEADS):
                dve.wait_ge(rs_psum, hd + 1)
                decay = cst[:, K_DECAY + 256 * hd:K_DECAY + 256 * hd + 256]
                dve.tensor_tensor(scored[:, hd, 0:256], ps[:, X + hd, 0:256], decay, ALU.mult)
                dve.tensor_tensor(scored[:, hd, 256:384], ps[:, X + hd, 256:384], decay[:, 0:128],
                                  ALU.mult).then_inc(rs_made, 1)
            splits_through(T_QS + LEAD)
            for hd in range(RET_HEADS):
                dve.wait_ge(ro_psum, hd + 1)
                for t in range(TT):
                    last = dve.bn_stats(bn[:, 2 * hd + t, 0:6], ps[:, X + hd, 256 * t:256 * t + 256])
                link(last)
                for t in range(TT):
                    last = dve.bn_aggr(mv[:, 2 + 2 * hd + t, :], bn[:, 2 * hd + t, 0:6])
                last.then_inc(ro_var, 1)
            for hd in range(RET_HEADS):
                dve.wait_ge(ro_var, hd + 1)
                dve.wait_ge(ro_dev, hd + 1)
                for t in range(TT):
                    c = 2 + 2 * hd + t
                    last = dve.tensor_scalar(ret[:, t, RET_DV * hd:RET_DV * hd + RET_DV],
                                             ps[:, X + hd, 256 * t:256 * t + 256], mv[:, c, 0:1], dev[:, c:c + 1],
                                             ALU.subtract, ALU.mult)
                last.then_inc(ret_normed, 1)
            splits_through(T_QS + 1 + LEAD)
            dve.wait_ge(ret_normed, 4)
            for t in range(TT):
                dve.wait_ge(silu_made, t + 1)
                dve.tensor_tensor(ret[:, t, :], ret[:, t, :], xn[:, t, :], ALU.mult).then_inc(ret_made, 1)

            def window_in(i):
                s = i % 2
                dve.wait_ge(win_psum, i + 1)
                if i >= 2:
                    dve.wait_ge(wint_psum, i - 1)
                else:
                    dve.wait_ge(ro_psum, 4)
                link(dve.scalar_tensor_tensor(win[:, s, :], cst[:, K_DIST:K_DIST + 384], -8.0 * SLOPES[i],
                                              ps[:, Y + s, 0:384], ALU.mult, ALU.add))
                dve.tensor_reduce(soft[:, s, 0:1], win[:, s, 0:128], AX_X, ALU.max)
                link(dve.tensor_reduce(soft[:, s, 1:2], win[:, s, 128:384], AX_X, ALU.max))
                dve.tensor_scalar(soft[:, s, 2:4], soft[:, s, 0:2], sink8[:, i:i + 1], -0.125, ALU.max,
                                  ALU.mult).then_inc(win_in, 1)

            def window_norm(i):
                s = i % 2
                dve.wait_ge(win_exp, i + 1)
                link(dve.tensor_tensor(soft[:, s, 8:10], soft[:, s, 4:6], soft[:, s, 6:8], ALU.add))
                link(dve.reciprocal(soft[:, s, 10:12], soft[:, s, 8:10]))
                for blk, (lo, hi) in enumerate(((0, 128), (128, 384))):
                    last = dve.tensor_scalar(win[:, s, lo:hi], win[:, s, lo:hi], soft[:, s, 10 + blk:11 + blk], None,
                                             ALU.mult)
                last.then_inc(win_made, 1)

            for i in range(SWA_HEADS + 1):
                if i == SWA_HEADS:
                    convert_transposed(C_RET, X)
                if i >= 1:
                    window_norm(i - 1)
                if i < SWA_HEADS:
                    if i == 3:
                        splits_through(T_GATER + 2 + LEAD)
                    window_in(i)
                if i == 6:
                    convert(C_SWA[0], ps[:, Y + 3, :], hidh[:, 0, :], hidl[:, 0, :])
                if i < 5 and i != 2:
                    splits_through(T_GATER + i + LEAD)
                if i in (6, 8):
                    splits_through(T_RET + i - 6)
            splits_through(T_RET + 3)
            convert(C_SWA[1], ps[:, Y + 3, :], hidh[:, 1, :], hidl[:, 1, :])
            splits_through(T_OUT2)
            for t in range(TT):
                dve.wait_ge(gates_made, 2 * t + 2)
                if t == 0:
                    dve.wait_ge(acc_done, A_YS + 1)
                else:
                    dve.wait_ge(tile_used, T_SWA + 2)
                dve.tensor_tensor(pair(xn, t), pair(sig_r, t), acc_pair(X, t), ALU.mult)
                link(dve.tensor_tensor(pair(sig_s, t), pair(sig_s, t), acc_pair(Y, t), ALU.mult))
                dve.tensor_tensor(xn[:, t, :], xn[:, t, :], sig_s[:, t, :], ALU.add).then_inc(merged_made, 1)
                splits_through(T_OUT2 + 3 * t)
                convert_tile(C_MERGED, X, t)
                splits_through(T_OUT2 + 2)
            boundary(7, T_FFN2, beside=False)
            ffn(2)
            for t in range(TT):
                add_to_h(8, t)

        @block.tensor
        def _(pe):
            def half_product(T, t, oph, opl, k0, acc, start=False, stop=False, signal=False, lap=0, step=None,
                             early=False):
                pe.wait_ge(low_made, T + 1 + 4 * lap)
                wh = high[:, T % RING, :].rearrange("p (k c) -> p k c", k=2)
                wl = low[:, T % RING, :].rearrange("p (k c) -> p k c", k=2)
                xs = slice(t * P, t * P + P)
                for banks in ((0,), (1,)) if step is not None or early else ((0, 1),):
                    if banks == (1,) and step is not None:
                        pe.wait_ge(actl_made, step)
                    for k in range(2):
                        for m, (op, w) in enumerate(((oph, wh), (oph, wl), (opl, wh))):
                            for n in banks:
                                last = pe.matmul(ps[:, acc + 2 * t + n, :], op[:, k0 + k, xs],
                                                 w[:, k, n * BANK:n * BANK + BANK],
                                                 start=(start and k == 0 and m == 0),
                                                 stop=(stop and k == 1 and m == 2))
                    if banks == (0,) and early:
                        last.then_inc(bank_done, 1)
                if t == 1:
                    last.then_inc(tile_used, 1)
                elif signal:
                    last.then_inc(acc_done, 1)

            def product(T, oph, opl, k0, acc, start=False, stop=False, signal=False, lap=0):
                for t in range(TT):
                    half_product(T, t, oph, opl, k0, acc, start, stop, signal, lap)

            def run(T, count, t, acc, oph=acth, opl=actl, lo=0, hi=None, signal=True, ready=None, steps=None,
                    early=False):
                for j in range(lo, count if hi is None else hi):
                    if ready:
                        pe.wait_ge(actl_made, ready + j + 1)
                    if steps is not None and j == lo:
                        pe.wait_ge(actl_made, steps + 2 * t + j // 2 + 1)
                    half_product(T + j, t, oph, opl, 2 * j, acc, start=(j == 0), stop=(j == count - 1),
                                 signal=(signal and j == count - 1),
                                 step=steps + 2 * t + 2 if steps is not None and j == 0 else None,
                                 early=(early and j == count - 1))

            def product_transposed(T, b, lap=0, steps=None):
                pe.wait_ge(low_made, T + 1 + 4 * lap)
                wh = high[:, T % RING, :].rearrange("p (k c) -> p k c", k=KT)
                wl = low[:, T % RING, :].rearrange("p (k c) -> p k c", k=KT)
                for m in range(2):
                    ms_ = slice(m * P, m * P + P)
                    for k in range(KT):
                        if steps is not None and m == 0 and k % 4 == 0:
                            pe.wait_ge(actl_made, steps + 3 + k // 4)
                        for n, (w, op) in enumerate(((wh, acth), (wh, actl), (wl, acth))):
                            last = pe.matmul(ps[:, b, 256 * m:256 * m + 256], w[:, k, ms_], op[:, k, :],
                                             start=(k == 0 and n == 0), stop=(k == KT - 1 and n == 2))
                last.then_inc(tile_used, 1)

            def transpose_tile(tok, acc, t, ready, value, made, halves=False):
                for b in range(2):
                    pe.wait_ge(ready, value - (1 - b if halves else 0))
                    for k in range(4):
                        f = (4 * b + k) * P
                        last = pe.transpose(ps[:, acc + 2 * t + b, k * P:k * P + P], tok[:, t, f:f + P], ident)
                    last.then_inc(made, 1)

            def turn(j, t):
                transpose_tile(xn, Y, t, xn_made, 4 * j + 2 * t + 2, xt_made, halves=True)

            def first_product(j, T, acc):
                run(T, 4, 0, acc, hi=3, steps=C_PRE[j])
                turn(j, 1)
                run(T, 4, 0, acc, lo=3)
                run(T, 4, 1, acc, steps=C_PRE[j])

            def up(T, half, n, lap=0, steps=None):
                if not isinstance(n, int) or n >= 2:
                    pe.wait_ge(relu_made, n - 1)
                product_transposed(T, X + half, lap, steps)

            def hid(x, half):
                return x[:, half, :].rearrange("p (k c) -> p k c", k=2)

            def down(T, half, n, start=False, lap=0):
                pe.wait_ge(hidl_made, n + 1)
                product(T, hid(hidh, half), hid(hidl, half), 0, Y, start, lap=lap)

            def ffn(f):
                T, n = FFN_TILES[f], 16 * f
                if f < 2:
                    pe.wait_ge(proj_made, 2 * f + 1)
                up(T, 0, n, steps=C_PRE[(1, 4, 7)[f]])
                up(T + 1, 1, n + 1)
                down(T + 2, 0, n, start=True)
                with pe.Fori(0, FFN_CHUNKS - 2) as lap:
                    up(T + 3, 0, n + 2 + 2 * lap, lap)
                    down(T + 4, 1, n + 1 + 2 * lap, lap=lap)
                    up(T + 5, 1, n + 3 + 2 * lap, lap)
                    down(T + 6, 0, n + 2 + 2 * lap, lap=lap)
                up(T + 27, 0, n + 14)
                down(T + 28, 1, n + 13)
                up(T + 29, 1, n + 15)
                for t in range(TT):
                    for half in range(2):
                        pe.wait_ge(hidl_made, n + 15 + half)
                        half_product(T + 30 + half, t, hid(hidh, half), hid(hidl, half), 0, Y, stop=half == 1,
                                     signal=half == 1, early=half == 1)

            def turn_p(layer, bank):
                pe.wait_ge(p_loaded, 16 * (layer + 1))
                for k in range(2):
                    for t in range(TT):
                        last = pe.transpose(ps[:, bank, 256 * k + P * t:256 * k + P * t + P],
                                            ptok[:, t, P * k:P * k + P], ident)
                last.then_inc(pt_made, 1)

            def to_ffn(j, layer, T):
                if layer is not None:
                    pe.wait_ge(actl_made, C_P[layer] + 1)
                    for t in range(TT):
                        run(T, 1, t, X, ph, pl)
                turn(j, 1)

            pe.wait_ge(ident_loaded, 16)
            turn(0, 0)
            run(T_V0, 4, 0, X, hi=2, steps=C_PRE[0])
            turn(0, 1)
            turn_p(0, Y)
            run(T_V0, 4, 0, X, lo=2, steps=C_PRE[0])
            run(T_V0, 4, 1, X, hi=2, steps=C_PRE[0])
            pe.wait_ge(ws_loaded, 32)
            for g in range(8):
                last = pe.transpose(ps[:, Y + 1 + g // 4, (g % 4) * P:(g % 4) * P + P], ws_raw[:, g, :], ident)
                if g % 4 == 3:
                    last.then_inc(wst_psum, 1)
            run(T_V0, 4, 1, X, lo=2, steps=C_PRE[0])
            pe.wait_ge(actl_made, C_P[0] + 1)
            pe.wait_ge(wst_made, 2)
            for j in range(2):
                product_transposed(T_U0 + j, Y + j)
            pe.wait_ge(v_normed, 2)
            for g in range(8):
                for n in range(TT):
                    c = (g % 2) * 256 + n * P
                    last = pe.matmul(ps[:, X + g // 2, c:c + P], v0[:, n, g * P:g * P + P], wst[:, g, :],
                                     start=True, stop=True)
                if g % 2:
                    last.then_inc(st_psum, 1)
            for j in range(2, 4):
                product_transposed(T_U0 + j, Y + j)
            run(T_OUT0, 4, 0, Y, ready=C_Y0, early=True)
            run(T_OUT0, 4, 1, Y, hi=3)
            turn(1, 0)
            run(T_OUT0, 4, 1, Y, lo=3, early=True)
            to_ffn(1, 0, T_PROJ0)
            ffn(0)
            turn(2, 0)
            turn_p(1, X + 2)
            first_product(2, T_GATE0, Y)
            turn(3, 0)
            first_product(3, T_Q, Y)

            def turn_heads(tok, acc, roped, made):
                pe.wait_ge(roped, 2)
                for hd in range(HEADS):
                    for t in range(TT):
                        c = (hd % 2) * 256 + t * P
                        last = pe.transpose(ps[:, acc + hd // 2, c:c + P], tok[:, t, hd * P:hd * P + P], ident)
                    if hd % 2:
                        last.then_inc(made, 1)

            run(T_K, 4, 0, X)
            turn_heads(qtok, Y, q_roped, qt_psum)
            run(T_K, 4, 1, X)

            def product_v(j):
                T, n = T_V + j, j // 2
                pe.wait_ge(low_made, T + 1)
                if n:
                    pe.wait_ge(v_copied, 1)
                wh = high[:, T % RING, :].rearrange("p (k c) -> p k c", k=4)
                wl = low[:, T % RING, :].rearrange("p (k c) -> p k c", k=4)
                for t in range(TT):
                    for k in range(4):
                        kk = 4 * (j % 2) + k
                        for m, (op, w) in enumerate(((acth, wh), (acth, wl), (actl, wh))):
                            last = pe.matmul(ps[:, Y + t, :], op[:, kk, t * P:t * P + P], w[:, k, :],
                                             start=(kk == 0 and m == 0), stop=(kk == KT - 1 and m == 2))
                last.then_inc(tile_used, 1)

            pe.wait_ge(qt_made, 4)
            product_v(0)
            turn_heads(xn, X, k_roped, kt_psum)
            product_v(1)
            pe.wait_ge(kt_made, 4)

            def scores(i):
                if i >= 2:
                    pe.wait_ge(prob_made, i - 1)
                for c in range(2):
                    b = X + 2 * (i % 2) + c
                    q, k = qt[64 * c:64 * c + 64, i, :], kt_[64 * c:64 * c + 64, i, :]
                    pe.matmul(ps[:, b, 0:128], q[:, 0:P], k[:, 0:P], start=True, stop=False)
                    pe.matmul(ps[:, b, 0:128], ident16[:, :], causal16[:, :], start=False, stop=True)
                    pe.matmul(ps[:, b, 128:384], q[:, P:2 * P], k, start=True, stop=False)
                    last = pe.matmul(ps[:, b, 256:384], ident16[:, :], causal16[:, :], start=False, stop=True)
                last.then_inc(score_psum, 1)

            def transpose_blocks(src, b, made):
                for blk in range(3):
                    last = pe.transpose(ps[:, b, blk * P:blk * P + P], src[:, blk * P:blk * P + P], ident)
                last.then_inc(made, 1)

            def attend(i):
                pe.wait_ge(attnt_made, i + 1)
                pe.wait_ge(v_copied, 1 + i // 4)
                b, at, vh = Y + 2 + i % 2, attnt[:, i % 2, :], v1[:, :, i * P:i * P + P]
                pe.matmul(ps[:, b, 0:P], at[:, 0:P], vh[:, 0], start=True, stop=True)
                pe.matmul(ps[:, b, P:2 * P], at[:, P:2 * P], vh[:, 0], start=True, stop=False)
                pe.matmul(ps[:, b, P:2 * P], at[:, 2 * P:3 * P], vh[:, 1], start=False, stop=True).then_inc(o_psum, 1)

            def turn_o(half):
                pe.wait_ge(o_normed, 4 * half + 4)
                for t in range(TT):
                    for k in range(4):
                        f = (4 * half + k) * P
                        last = pe.transpose(ps[:, (X if half else Y) + t, k * P:k * P + P], o1[:, t, f:f + P], ident)
                    last.then_inc(o_trans, 1)

            for i in range(HEADS + 3):
                if i < HEADS:
                    scores(i)
                if i == 1:
                    product_v(2)
                if 2 <= i <= HEADS + 1:
                    pe.wait_ge(attn_made, i - 1)
                    if i >= 4:
                        pe.wait_ge(o_copied, i - 3)
                    transpose_blocks(attn[:, i % 2, :], Y + 2 + i % 2, attnt_psum)
                if i == 2:
                    product_v(3)
                if i >= 3:
                    attend(i - 3)
                if i == HEADS + 1:
                    pe.wait_ge(v_copied, 2)
                    turn_o(0)
            pe.wait_ge(actl_made, C_O1 + 2)
            half_product(T_WO, 0, acth, actl, 0, Y, start=True)
            pe.wait_ge(o_copied, HEADS)
            half_product(T_WO, 1, acth, actl, 0, Y, start=True)
            turn_o(1)
            run(T_WO, 4, 0, Y, lo=1, hi=2)
            pe.wait_ge(actl_made, C_O1 + 4)
            run(T_WO, 4, 0, Y, lo=2, early=True)
            run(T_WO, 4, 1, Y, lo=1, hi=3)
            turn(4, 0)
            run(T_WO, 4, 1, Y, lo=3, early=True)
            to_ffn(4, 1, T_PROJ1)
            ffn(1)
            turn(5, 0)
            first_product(5, T_GATE1, Y)
            turn(6, 0)
            first_product(6, T_VR, Y)

            for t in range(TT):
                run(T_GR, 4, t, X)
            pe.wait_ge(vr_made, 2)
            for j in range(4):
                product_transposed(T_QR + j, Y + j)
            pe.wait_ge(silu_made, 2)
            pe.wait_ge(qrt_made, 4)
            for hd in range(RET_HEADS):
                pe.matmul(ps[:, X + hd, 0:256], krt[:, hd, 0:P], qrt[:, hd, :], start=True, stop=True)
                pe.matmul(ps[:, X + hd, 256:384], krt[:, hd, P:2 * P], qrt[:, hd, P:2 * P], start=True,
                          stop=True).then_inc(rs_psum, 1)
            product_transposed(T_QS, Y)
            for hd in range(RET_HEADS):
                pe.wait_ge(rs_made, hd + 1)
                sc, vh = scored[:, hd, :], vr[:, :, RET_DV * hd:RET_DV * hd + RET_DV]
                pe.matmul(ps[:, X + hd, 0:256], sc[:, 0:P], vh[:, 0], start=True, stop=True)
                pe.matmul(ps[:, X + hd, 256:512], sc[:, P:2 * P], vh[:, 0], start=True, stop=False)
                pe.matmul(ps[:, X + hd, 256:512], sc[:, 2 * P:3 * P], vh[:, 1], start=False,
                          stop=True).then_inc(ro_psum, 1)
            product_transposed(T_QS + 1, Y + 1)
            product_transposed(T_KVS, Y + 2)

            def window_scores(i):
                g, half = i // 4, i % 2
                if i >= 2:
                    pe.wait_ge(win_in, i - 1)
                q = qst[64 * half:64 * half + 64, i // 2, :]
                k = kst[64 * half:64 * half + 64, g, :]
                pe.matmul(ps[:, Y + i % 2, 0:128], q[:, 0:P], k[:, 0:P], start=True, stop=True)
                pe.matmul(ps[:, Y + i % 2, 128:384], q[:, P:2 * P], k, start=True, stop=True).then_inc(win_psum, 1)

            def window_attend(i):
                g, half, c = i // 4, i % 2, ((i // 2) % 2) * 256
                pe.wait_ge(wint_made, i + 1)
                if i == 4:
                    pe.wait_ge(actl_made, C_SWA[0] + 1)
                o, wt = ps[64 * half:64 * half + 64, Y + 3, :], wint[:, i % 2, :]
                v_0, v_1 = vs[:, 0, 64 * g:64 * g + 64], vs[:, 1, 64 * g:64 * g + 64]
                pe.matmul(o[:, c:c + P], v_0, wt[:, 0:P], start=True, stop=True)
                pe.matmul(o[:, c + P:c + 2 * P], v_0, wt[:, P:2 * P], start=True, stop=False)
                pe.matmul(o[:, c + P:c + 2 * P], v_1, wt[:, 2 * P:3 * P], start=False, stop=True).then_inc(wo_psum, 1)

            def window_turn(i):
                pe.wait_ge(win_made, i + 1)
                if i >= 1:
                    pe.wait_ge(wint_made, i)
                transpose_blocks(win[:, i % 2, :], Y + 2, wint_psum)

            def stage(i):
                if i < SWA_HEADS:
                    window_scores(i)
                if 2 <= i <= SWA_HEADS + 1:
                    window_turn(i - 2)
                if i >= 3:
                    window_attend(i - 3)

            pe.wait_ge(ret_normed, 4)
            for gate, T in enumerate((T_GATER, T_GATES)):
                for i in range(2):
                    for t in range(TT):
                        if gate and i == 0:
                            pe.wait_ge(sigr_copied, t + 1)
                        half_product(T + i, t, acth, actl, 2 * i, X, start=(i == 0))
                    if gate == 0 and i == 0:
                        pe.wait_ge(kv_made, 1)
                        for t in range(TT):
                            last = pe.transpose(ps[:, Y + 3, t * P:t * P + P], kvt[:, 1, t * P:t * P + P], ident)
                        last.then_inc(vs_psum, 1)
                        pe.wait_ge(qs_made, 2)
                        pe.wait_ge(ks_moved, 64)
                        pe.wait_ge(vs_made, 1)
                    stage(4 * gate + i)
                for t in range(TT):
                    run(T, 4, t, X, lo=2)
                    stage(4 * gate + 2 + t)
            transpose_tile(ret, X, 0, sigs_copied, 1, ret_trans)
            transpose_tile(ret, X, 1, sigs_copied, 2, ret_trans)
            stage(SWA_HEADS)
            run(T_RET, 4, 0, X, signal=False, hi=1, steps=C_RET)
            stage(SWA_HEADS + 1)
            run(T_RET, 4, 0, X, signal=False, lo=1, hi=3, steps=C_RET)
            stage(SWA_HEADS + 2)
            run(T_RET, 4, 0, X, signal=False, lo=3)
            run(T_RET, 4, 1, X, signal=False, hi=3, steps=C_RET)
            swah = hidh[:, :, :].rearrange("p b (k c) -> p (b k) c", k=2)
            swal = hidl[:, :, :].rearrange("p b (k c) -> p (b k) c", k=2)
            pe.wait_ge(actl_made, C_SWA[1] + 1)
            run(T_SWA, 2, 0, Y, swah, swal)
            run(T_RET, 4, 1, X, signal=False, lo=3)
            run(T_SWA, 2, 1, Y, swah, swal, hi=1)
            transpose_tile(xn, X, 0, merged_made, 1, merged_trans)
            run(T_SWA, 2, 1, Y, swah, swal, lo=1)
            run(T_OUT2, 4, 0, Y, hi=3, steps=C_MERGED)
            transpose_tile(xn, X, 1, merged_made, 2, merged_trans)
            run(T_OUT2, 4, 0, Y, lo=3, early=True)
            run(T_OUT2, 4, 1, Y, hi=3, steps=C_MERGED)
            turn(7, 0)
            run(T_OUT2, 4, 1, Y, lo=3, early=True)
            to_ffn(7, None, None)
            ffn(2)


def constants():
    import numpy as np

    c = np.zeros((P, K_END), np.float32)
    i, j = np.arange(P)[:, None], np.arange(P)[None, :]
    c[:, K_ID:K_ID + P] = np.eye(P)
    far = 1e30
    own = np.where(i >= j, i - j, far)
    before = np.where(i + P - j < P, i + P - j, far)
    c[:, K_DIST:K_DIST + 384] = np.concatenate([own, before, own], axis=1)
    c[:, K_TRIU:K_TRIU + P] = i <= j
    log_gamma = np.log(np.float32(1.0) - np.exp2(np.float32(-5.0) - np.arange(RET_HEADS, dtype=np.float32)))
    diff = (np.arange(2 * P)[None, :] - i).astype(np.float32)
    for hd in range(RET_HEADS):
        d = np.where(diff >= 0, np.exp(log_gamma[hd] * np.maximum(diff, 0)), 0.0) * P ** -0.5
        c[:, K_DECAY + 256 * hd:K_DECAY + 256 * hd + 256] = d
    freq = np.float32(500000.0) ** (-(np.arange(0, ROT, 2, dtype=np.float32) / ROT))
    c[:, K_FREQ:K_FREQ + 8] = freq[None, :]
    return c


def kernel(**inputs):
    import numpy as np
    import concourse.bacc as bacc
    from concourse.bass_utils import run_bass_kernel_spmd

    nc = bacc.Bacc("TRN2", target_bir_lowering=False, num_devices=1)
    arrays, args = {}, {}
    for name, value in {**inputs, "consts": constants()}.items():
        v = np.ascontiguousarray(value)
        arrays[f"in_{name}"] = v
        args[name] = nc.dram_tensor(f"in_{name}", v.shape, mybir.dt.from_np(v.dtype), kind="ExternalInput").ap()
    out = nc.dram_tensor("out_h", (1, SEQ, D), F32, kind="ExternalOutput").ap()
    build(nc, args, out)
    r = run_bass_kernel_spmd(nc, [arrays], core_ids=[0])
    return r.results[0]["out_h"]
```
